# Optimizing a Trainium2 kernel written in Bass

```python
import math
import jax, jax.numpy as jnp
from jax import lax
import numpy as np

D_MODEL = 1024
BATCH = 1
SEQ = 1024
DEPTH = 1

HEAD_DIM = 64
DSA_HEADS = 8
IDX_HEADS = 8
IDX_DIM = 64
TOPK_MAX = 256
SWA_HEADS = 8
SWA_KV_HEADS = 2
WINDOW = 128
BLOCK = 128
MEM_TOKENS = 256
MEM_HEADS = 4
MEM_HEAD_DIM = D_MODEL // MEM_HEADS
D_MIX = (DSA_HEADS + SWA_HEADS) * HEAD_DIM
D_FF = 4 * D_MODEL
ROPE_THETA = 10000.0
LN_EPS = 1e-5
DEEPNORM_ALPHA = (2.0 * DEPTH) ** 0.25
DEEPNORM_BETA = (8.0 * DEPTH) ** -0.25
IN_SIZES = (DSA_HEADS * HEAD_DIM, HEAD_DIM, HEAD_DIM,
            IDX_HEADS * IDX_DIM, IDX_DIM, IDX_HEADS,
            SWA_HEADS * HEAD_DIM, SWA_KV_HEADS * HEAD_DIM, SWA_KV_HEADS * HEAD_DIM)
IN_COLS = sum(IN_SIZES)

kernel_name = "hymba_dsa_swa_sink_deepnorm_layer"

def layer_norm(x, g, b):
    xf = x.astype(jnp.float32)
    mu = jnp.mean(xf, axis=-1, keepdims=True)
    var = jnp.mean(jnp.square(xf - mu), axis=-1, keepdims=True)
    y = (xf - mu) * lax.rsqrt(var + LN_EPS)
    return (y * g.astype(jnp.float32) + b.astype(jnp.float32)).astype(x.dtype)

def rope_tables(positions, dim):
    inv = ROPE_THETA ** (-jnp.arange(0, dim, 2, dtype=jnp.float32) / dim)
    ang = positions.astype(jnp.float32)[..., None] * inv
    return jnp.cos(ang), jnp.sin(ang)

def apply_rope(x, cos, sin):
    half = x.shape[-1] // 2
    xf = x.astype(jnp.float32)
    x1, x2 = xf[..., :half], xf[..., half:]
    c, s = cos[:, :, None, :], sin[:, :, None, :]
    return jnp.concatenate([x1 * c - x2 * s, x2 * c + x1 * s], axis=-1).astype(x.dtype)

def dsa_sparse_attention(q, k, v, iq, ik, iw):
    B, S, H, dh = q.shape
    n_sel = min(TOPK_MAX, S // 4)
    nb = S // BLOCK
    key_pos = jnp.arange(S)
    scale = HEAD_DIM ** -0.5
    idx_scale = (IDX_DIM ** -0.5) * (IDX_HEADS ** -0.5)

    def to_blocks(a):
        return jnp.moveaxis(a.reshape((B, nb, BLOCK) + a.shape[2:]), 1, 0)

    def one_block(args):
        qb, iqb, iwb, start = args
        qpos = start + jnp.arange(BLOCK)
        causal = key_pos[None, :] <= qpos[:, None]
        rel = jax.nn.relu(jnp.einsum('bthd,bsd->bths', iqb, ik).astype(jnp.float32))
        score = jnp.einsum('bths,bth->bts', rel, iwb.astype(jnp.float32)) * idx_scale
        score = jnp.where(causal[None], score, -jnp.inf)
        _, sel = lax.top_k(score, n_sel)
        valid = sel <= qpos[None, :, None]
        k_sel = jax.vmap(lambda kb, ib: kb[ib])(k, sel)
        v_sel = jax.vmap(lambda vb, ib: vb[ib])(v, sel)
        logits = jnp.einsum('bthd,btnd->bthn', qb, k_sel).astype(jnp.float32) * scale
        logits = jnp.where(valid[:, :, None, :], logits, -jnp.inf)
        p = jax.nn.softmax(logits, axis=-1).astype(v.dtype)
        return jnp.einsum('bthn,btnd->bthd', p, v_sel)

    starts = jnp.arange(nb) * BLOCK
    out = lax.map(one_block, (to_blocks(q), to_blocks(iq), to_blocks(iw), starts))
    return jnp.moveaxis(out, 0, 1).reshape(B, S, H * dh)

def swa_sink_attention(q, k, v, sinks):
    B, S, Hq, dh = q.shape
    Hkv = k.shape[2]
    G = Hq // Hkv
    nb = S // BLOCK
    scale = dh ** -0.5
    qb = q.reshape(B, nb, BLOCK, Hkv, G, dh)

    def band(a):
        ab = a.reshape(B, nb, BLOCK, Hkv, dh)
        prev = jnp.pad(ab, ((0, 0), (1, 0), (0, 0), (0, 0), (0, 0)))[:, :-1]
        return jnp.concatenate([prev, ab], axis=2)

    kb, vb = band(k), band(v)
    qpos = jnp.arange(BLOCK)[:, None] + BLOCK
    kpos = jnp.arange(2 * BLOCK)[None, :]
    diff = qpos - kpos
    inband = (diff >= 0) & (diff < WINDOW)
    first = (jnp.arange(nb)[:, None, None] == 0) & (kpos[None] < BLOCK)
    valid = inband[None] & jnp.logical_not(first)
    logits = jnp.einsum('bnqhgd,bnkhd->bnhgqk', qb, kb).astype(jnp.float32) * scale
    logits = jnp.where(valid[None, :, None, None], logits, -jnp.inf)
    sink = jnp.broadcast_to(sinks.astype(jnp.float32).reshape(1, 1, Hkv, G, 1, 1),
                            logits.shape[:-1] + (1,))
    p = jax.nn.softmax(jnp.concatenate([logits, sink], axis=-1), axis=-1)[..., :-1]
    out = jnp.einsum('bnhgqk,bnkhd->bnqhgd', p.astype(v.dtype), vb)
    return out.reshape(B, S, Hq * dh)

def memory_cross_attention(x, mem, wq, wk, wv, wo):
    B, S, _ = x.shape
    M = mem.shape[1]
    q = (x @ wq).reshape(B, S, MEM_HEADS, MEM_HEAD_DIM)
    k = (mem @ wk).reshape(B, M, MEM_HEADS, MEM_HEAD_DIM)
    v = (mem @ wv).reshape(B, M, MEM_HEADS, MEM_HEAD_DIM)
    logits = jnp.einsum('bshd,bmhd->bhsm', q, k).astype(jnp.float32) * (MEM_HEAD_DIM ** -0.5)
    p = jax.nn.softmax(logits, axis=-1).astype(v.dtype)
    o = jnp.einsum('bhsm,bmhd->bshd', p, v).reshape(B, S, MEM_HEADS * MEM_HEAD_DIM)
    return o @ wo

def squared_relu_mlp(x, w_up, w_down):
    return jnp.square(jax.nn.relu(x @ w_up)) @ w_down

def setup_inputs(seed: int = 0) -> dict:
    key = jax.random.key(seed)
    ks = jax.random.split(key, 20)
    f32 = jnp.float32
    n = lambda k, shape, s: jax.random.normal(k, shape, f32) * s
    x = n(ks[0], (BATCH, SEQ, D_MODEL), 1.0)
    mem = n(ks[1], (BATCH, MEM_TOKENS, D_MODEL), 1.0)
    positions = jnp.broadcast_to(jnp.arange(SEQ, dtype=jnp.int32)[None, :], (BATCH, SEQ))
    return {
        "x": x,
        "mem": mem,
        "positions": positions,
        "w_in": n(ks[2], (DEPTH, D_MODEL, IN_COLS), D_MODEL ** -0.5),
        "b_in": n(ks[3], (DEPTH, IN_COLS), 0.01),
        "swa_sinks": n(ks[4], (DEPTH, SWA_HEADS), 0.5),
        "w_o": n(ks[5], (DEPTH, D_MIX, D_MODEL), D_MIX ** -0.5 * DEEPNORM_BETA),
        "ln1_g": 1.0 + n(ks[6], (DEPTH, D_MODEL), 0.02),
        "ln1_b": n(ks[7], (DEPTH, D_MODEL), 0.02),
        "wq_mem": n(ks[8], (DEPTH, D_MODEL, D_MODEL), D_MODEL ** -0.5),
        "wk_mem": n(ks[9], (DEPTH, D_MODEL, D_MODEL), D_MODEL ** -0.5),
        "wv_mem": n(ks[10], (DEPTH, D_MODEL, D_MODEL), D_MODEL ** -0.5),
        "wo_mem": n(ks[11], (DEPTH, D_MODEL, D_MODEL), D_MODEL ** -0.5 * DEEPNORM_BETA),
        "ln2_g": 1.0 + n(ks[12], (DEPTH, D_MODEL), 0.02),
        "ln2_b": n(ks[13], (DEPTH, D_MODEL), 0.02),
        "w_up": n(ks[14], (DEPTH, D_MODEL, D_FF), D_MODEL ** -0.5 * DEEPNORM_BETA),
        "w_down": n(ks[15], (DEPTH, D_FF, D_MODEL), D_FF ** -0.5 * DEEPNORM_BETA),
        "ln3_g": 1.0 + n(ks[16], (DEPTH, D_MODEL), 0.02),
        "ln3_b": n(ks[17], (DEPTH, D_MODEL), 0.02),
    }

def reference(x, mem, positions, w_in, b_in, swa_sinks, w_o, ln1_g, ln1_b,
              wq_mem, wk_mem, wv_mem, wo_mem, ln2_g, ln2_b,
              w_up, w_down, ln3_g, ln3_b):
    B, S, _ = x.shape
    cos, sin = rope_tables(positions, HEAD_DIM)
    offsets = np.cumsum(IN_SIZES)[:-1].tolist()
    h = x
    for l in range(DEPTH):
        proj = h @ w_in[l] + b_in[l]
        dq, dk, dv, iq, ik, iw, sq, sk, sv = jnp.split(proj, offsets, axis=-1)
        dq = apply_rope(dq.reshape(B, S, DSA_HEADS, HEAD_DIM), cos, sin)
        dk = apply_rope(dk.reshape(B, S, 1, HEAD_DIM), cos, sin)[:, :, 0]
        iq = apply_rope(iq.reshape(B, S, IDX_HEADS, IDX_DIM), cos, sin)
        ik = apply_rope(ik.reshape(B, S, 1, IDX_DIM), cos, sin)[:, :, 0]
        o_dsa = dsa_sparse_attention(dq, dk, dv, iq, ik, iw)
        sq = apply_rope(sq.reshape(B, S, SWA_HEADS, HEAD_DIM), cos, sin)
        sk = apply_rope(sk.reshape(B, S, SWA_KV_HEADS, HEAD_DIM), cos, sin)
        sv = sv.reshape(B, S, SWA_KV_HEADS, HEAD_DIM)
        o_swa = swa_sink_attention(sq, sk, sv, swa_sinks[l])
        mix = jnp.concatenate([o_dsa, o_swa], axis=-1) @ w_o[l]
        h = layer_norm(DEEPNORM_ALPHA * h + mix, ln1_g[l], ln1_b[l])
        c = memory_cross_attention(h, mem, wq_mem[l], wk_mem[l], wv_mem[l], wo_mem[l])
        h = layer_norm(DEEPNORM_ALPHA * h + c, ln2_g[l], ln2_b[l])
        m = squared_relu_mlp(h, w_up[l], w_down[l])
        h = layer_norm(DEEPNORM_ALPHA * h + m, ln3_g[l], ln3_b[l])
    return h


_drawn_inputs = setup_inputs


def setup_inputs(seed=0):
    import zlib

    import numpy as np

    out = dict(_drawn_inputs(seed))
    spreads = {}
    factors = {'b_in': 8.0,
     'swa_sinks': 8.0,
     'ln1_g': 2.723,
     'ln1_b': 2.851,
     'ln2_g': 7.972,
     'ln2_b': 7.419,
     'ln3_g': 8.168,
     'ln3_b': 8.213}
    for name, (base, spread) in spreads.items():
        noise = np.random.default_rng([zlib.crc32(name.encode()), seed]).standard_normal(out[name].shape)
        drawn = base * np.exp(spread * noise) if base else spread * noise
        out[name] = __import__('jax').numpy.asarray(drawn.astype(out[name].dtype))
    for name, factor in factors.items():
        out[name] = (out[name] * factor).astype(out[name].dtype)
    return out
```

```python
import numpy as np
import concourse.bass as bass
from concourse import mybir
from concourse.alu_op_type import AluOpType as ALU
from contextlib import ExitStack

F32 = mybir.dt.float32
F32R = mybir.dt.float32r
I32 = mybir.dt.int32
ACT = mybir.ActivationFunctionType
AX = mybir.AxisListType

P = 128
SEQ = 1024
D = 1024
FF = 4096
HEAD = 64
HEADS = 8
MEM = 256
MEM_HEADS = 4
MEM_HEAD = D // MEM_HEADS
TOPK = 256
NT = SEQ // P
NK = D // P
HALF = 512
ALPHA = 2.0 ** 0.25
LN_EPS = 1e-5
SCALE = HEAD ** -0.5
MEM_SCALE = MEM_HEAD ** -0.5
IDX_SCALE = (HEAD ** -0.5) * (HEADS ** -0.5)
MASKED = -1.0e30
TAKEN = -3.0e38
FIRST_TOPK_TILE = TOPK // P

V_COLS = HEADS + HEAD + 2 * HEAD
CHUNK = 2048
C_V, C_K, C_IQ, C_DQ, C_SQ = 0, 1, 2, 4, 6
C_MEM = 8
C_MIX = C_MEM + 4 * MEM_HEADS
C_G = C_MIX + 4
C_U = C_G + 4
C_MLP = C_U + 4
N_FF = FF // 256
N_CHUNKS = C_MLP + 2 * N_FF

TWO_PI = 2.0 * np.pi
PI_A = 6.28125
PI_B = float(np.float32(np.round((TWO_PI - PI_A) * 2 ** 20) / 2 ** 20))
PI_C = float(np.float32(TWO_PI - PI_A - PI_B))
ROUND = 1.5 * 2.0 ** 23
PI_DOWN = float(np.nextafter(np.float32(np.pi), np.float32(0)))


def rope_units():
    units = []
    for j, what in enumerate(("dkik", "sk")):
        units += [(C_K, j, (what, 0), hf) for hf in range(2)]
    for chunk, what in ((C_IQ, "iq"), (C_DQ, "dq"), (C_SQ, "sq")):
        for m in range(4):
            units += [(chunk + m // 2, m % 2, (what, m), hf) for hf in range(2)]
    return units


ROPE = rope_units()
N_ROPE_FIRST = 4 + 8
BIAS_COLUMN = {("dkik", 0): 0, ("sk", 0): 1}
for _m in range(4):
    BIAS_COLUMN[("iq", _m)] = 2 + _m
    BIAS_COLUMN[("dq", _m)] = 6 + _m
    BIAS_COLUMN[("sq", _m)] = 10 + _m

HEAD_ROW = {"keys": 0, "iq": 2 * P, "D": 6 * P, "S": 10 * P}

IDX = [(i, h) for i in range(FIRST_TOPK_TILE, NT) for h in range(HEADS)]
ATT = [("S", i, h) for i in range(NT) for h in range(HEADS)]
ATT += [("D", i, h) for i in range(NT) for h in range(HEADS)]


def keys_of(unit):
    kind, i, _ = unit
    if kind == "D":
        return 0, i + 1
    return (i - 1, 2) if i else (0, 1)


A_ROPE = 0
A_MEM = A_ROPE + len(ROPE)
A_ATT = A_MEM + 10 * MEM_HEADS
A_UP = A_ATT + 2 * NT
L_IDX = 0
L_ATT = L_IDX + len(IDX)
L_GEMM = L_ATT + len(ATT)
L_DOWN = L_GEMM + 3 * 2 * NT
T_ROT = 0
T_ATT = []
_n = T_ROT + len(ROPE)
for _u in ATT:
    T_ATT.append(_n)
    _n += (keys_of(_u)[1] + 3) // 4
T_O = _n
T_STAGE = T_O + 2 * NT


def last_uses():
    last = {}
    for r, (c, _, _, _) in enumerate(ROPE):
        last[c] = ("A", A_ROPE + r)
    for h in range(MEM_HEADS):
        for what, use in enumerate((0, 1, 5, 9)):
            last[C_MEM + 4 * h + what] = ("A", A_MEM + 10 * h + use)
    for n in range(12):
        stage, ch = divmod(n // 2, 2)
        last[C_MIX + n] = ("L", L_GEMM + 16 * stage + 8 * ch + NT - 1)
    for f in range(N_FF):
        last[C_MLP + 2 * f] = ("A", A_UP + 4 * f + 3)
        last[C_MLP + 2 * f + 1] = ("L", L_DOWN + 8 * f + 7)
    return last


LAST_USE = last_uses()
N_GEMM = 3 * 2 * NT


def transposed_at(g):
    stage, t = divmod(g - NT - 2, 2 * NT)
    return (stage, t) if 0 <= stage < 3 and 0 <= t < NT else None


def build_layer(nc, a):
    def place(name, shape, dtype, kb):
        return nc.alloc_sbuf_tensor_at(name, shape, dtype, offset=base + int(kb * 1024))

    base = (nc.sbuf_base + 63) // 64 * 64
    ctx = ExitStack()
    with ctx:
        def sem(name):
            return ctx.enter_context(nc.semaphore(name))

        def sems(name, n):
            return [sem(f"{name}{i}") for i in range(n)]

        raw = [place(f"raw{s}", [P, CHUNK], F32, 8 * s) for s in range(2)]
        w_at = [16, 32, 80, 96]
        w_hi = [place(f"w_hi{s}", [P, CHUNK], F32R, w_at[s]) for s in range(4)]
        w_lo = [place(f"w_lo{s}", [P, CHUNK], F32R, w_at[s] + 8) for s in range(4)]

        x_hi = place("x_hi", [P, NK, SEQ], F32R, 48)
        x_lo = place("x_lo", [P, NK, SEQ], F32R, 80)
        h_buf = place("h_buf", [P, NT, D], F32, 48)
        mem_hi = place("mem_hi", [P, NK, MEM], F32R, 80)
        mem_lo = place("mem_lo", [P, NK, MEM], F32R, 88)
        logit = [place(f"logit{s}", [P, SEQ], F32, 96 + 4 * s) for s in range(2)]
        prob_t = [place(f"prob_t{s}", [P, SEQ], F32, 104 + 4 * s) for s in range(2)]

        key_hi = [place(f"key_hi{j}", [P, SEQ], F32R, 112 + 8 * j) for j in range(4)]
        key_lo = [place(f"key_lo{j}", [P, SEQ], F32R, 116 + 8 * j) for j in range(4)]
        q_tile = [place(f"q_tile{s}", [P, HEADS, P], F32R, 144 + 4 * s) for s in range(3)]
        roped = [place(f"roped{s}", [P, HALF], F32, 156 + 2 * s) for s in range(2)]
        score, at = {}, 160.0
        for i in range(FIRST_TOPK_TILE, NT):
            score[i] = place(f"score{i}", [P, (i + 1) * P], F32, at)
            at += (i + 1) * P * 4 / 1024
        x_raw = [place(f"x_raw{k}", [P, SEQ], F32, (128 if k < 4 else 160) + 4 * (k % 4))
                 for k in range(NK)]
        mem_raw = place("mem_raw", [P, NK, MEM], F32, 48)
        pos_i = place("pos_i", [P, SEQ], I32, 144)
        angle = place("angle", [P, SEQ], F32, 112)
        turns = place("turns", [P, SEQ], F32, 116)
        b_v = place("b_v", [P, V_COLS], F32, 120)
        act_hi = place("act_hi", [P, NT, NK, P], F32R, 112)
        act_lo = place("act_lo", [P, NT, NK, P], F32R, 144)

        v_all = place("v_all", [P, NT, V_COLS], F32, 176.5)
        cos = place("cos", [P, SEQ], F32, 183)
        sin = place("sin", [P, SEQ], F32, 187)
        q_raw = [place(f"q_raw{s}", [P, HALF], F32, 191 + 2 * s) for s in range(2)]
        rot_part = place("rot_part", [P, HALF], F32, 195)
        prob = [place(f"prob{s}", [P, SEQ], F32, 183 + 4 * s) for s in range(2)]
        kv_hi = [place(f"kv_hi{s}", [P, 2, MEM], F32R, 191 + 4 * s) for s in range(2)]
        kv_lo = [place(f"kv_lo{s}", [P, 2, MEM], F32R, 193 + 4 * s) for s in range(2)]
        stage_out = [place(f"stage_out{s}", [P, HALF], F32, 199 + 2 * s) for s in range(2)]
        q_hi = [place(f"q_hi{s}", [P, HALF], F32R, 199 + 2 * s) for s in range(2)]
        neg_max = place("neg_max", [P, len(ATT)], F32, 203)
        sums = place("sums", [P, len(ATT)], F32, 203.5)
        m8 = [place(f"m8_{s}", [P, 8], F32, 204 + s / 16) for s in range(2)]
        sink_exp = place("sink_exp", [P, HEADS], F32, 204.125)
        inv_sum = place("inv_sum", [P, HEADS], F32, 204.1875)

        p_store = place("p_store", [P, NT, HALF], F32, 176.5)
        gamma = place("gamma", [P, D], F32, 192.5)
        beta = place("beta", [P, D], F32, 196.5)
        x_res = [place(f"x_res{s}", [P, HALF], F32, 200.5 + 2 * s) for s in range(2)]
        p_work = [place(f"p_work{s}", [P, HALF], F32, 200.5 + 2 * s) for s in range(2)]
        hid_hi = [place(f"hid_hi{s}", [P, 2, HALF], F32R, 176.5 + 8 * s) for s in range(2)]
        hid_lo = [place(f"hid_lo{s}", [P, 2, HALF], F32R, 180.5 + 8 * s) for s in range(2)]
        relu_buf = [place(f"relu_buf{s}", [P, HALF], F32, 200.5 + 2 * s) for s in range(2)]

        ident = place("ident", [P, P], F32, 204.5)
        rot = place("rot", [P, P], F32, 205)
        swa_mask = place("swa_mask", [P, 2 * P], F32, 205.5)
        causal = place("causal", [P, 2 * P], F32, 206.5)
        bias_qk = place("bias_qk", [P, 14], F32, 207.5)
        sinks = place("sinks", [P, HEADS], F32, 207.5625)
        neg_sinks = place("neg_sinks", [P, HEADS], F32, 207.59375)
        inv_freq = place("inv_freq", [P, 1], F32, 207.625)
        eps = place("eps", [P, 1], F32, 207.65625)
        bn = [place(f"bn{s}", [P, 2, 6], F32, 205.5 + s / 16) for s in range(2)]
        mean_var = [place(f"mean_var{s}", [P, 2], F32, 205.625 + s / 32) for s in range(2)]
        std = [place(f"std{s}", [P, 1], F32, 205.6875 + s / 32) for s in range(2)]
        var_eps = place("var_eps", [P, 1], F32, 205.75)
        rstd0 = place("rstd0", [P, 1], F32, 205.78125)
        newton = place("newton", [P, 1], F32, 205.8125)
        newton2 = place("newton2", [P, 1], F32, 205.84375)
        rstd = place("rstd", [P, 1], F32, 205.875)
        mem_max = [place(f"mem_max{s}", [P, 2], F32, 205.90625 + s / 32) for s in range(2)]
        mem_bias = [place(f"mem_bias{s}", [P, 2], F32, 205.96875 + s / 32) for s in range(2)]
        mem_sum = [place(f"mem_sum{s}", [P, 2], F32, 206.03125 + s / 32) for s in range(2)]
        mem_inv = place("mem_inv", [P, 2], F32, 206.09375)

        ring_l = [ctx.enter_context(nc.psum_tensor(f"ring_l{s}", [P, 2 * HALF], F32)) for s in range(2)]
        ring_t = [ctx.enter_context(nc.psum_tensor(f"ring_t{s}", [P, HALF], F32)) for s in range(2)]
        ring_a = [ctx.enter_context(nc.psum_tensor(f"ring_a{s}", [P, HALF], F32)) for s in range(2)]
        l_full, l_free = sems("l_full", 2), sems("l_free", 2)
        t_full, t_free = sems("t_full", 2), sems("t_free", 2)
        a_full, a_free = sems("a_full", 2), sems("a_free", 2)

        def freed(eng, sem2, n):
            if n >= 2:
                eng.wait_ge(sem2[n % 2], n // 2)

        def filled(eng, sem2, n):
            eng.wait_ge(sem2[n % 2], n // 2 + 1)

        def emptied(eng, sem2, n):
            eng.wait_ge(sem2[n % 2], n // 2 + 1)

        def chunk_used(eng, c):
            if c == C_V:
                eng.wait_ge(v_full, NT)
                return
            ring, n = LAST_USE[c]
            filled(eng, a_full if ring == "A" else l_full, n)

        def multiplied(eng, n):
            if n % HEADS == HEADS - 1:
                filled(eng, a_full, A_ATT + n // HEADS)
            else:
                eng.wait_ge(pv_done, n // HEADS * (HEADS - 1) + n % HEADS + 1)

        v_bank = [ring_a[0], ring_a[1], ring_t[0], ring_t[1], ring_l[0][:, 0:HALF], ring_l[0][:, HALF:],
                  ring_l[1][:, 0:HALF], ring_l[1][:, HALF:]]
        v_full = sem("v_full")
        v_done = sem("v_done")
        q_rounded = sem("q_rounded")
        q_split = sem("q_split")
        qk_stored = sems("qk_stored", 2)
        keys_in = sem("keys_in")
        q_in = sems("q_in", 3)
        consts_in = sem("consts_in")
        pos_in = sem("pos_in")
        mem_in = sem("mem_in")
        x_in = sems("x_in", NK)
        x_hi_done = sem("x_hi_done")
        x_lo_done = sem("x_lo_done")
        mem_hi_done = sem("mem_hi_done")
        mem_lo_done = sem("mem_lo_done")
        raw_in = sems("raw_in", 2)
        w_rounded = sem("w_rounded")
        w_ready = sem("w_ready")
        trig_steps = sem("trig_steps")
        trig_done = sem("trig_done")
        rope_done = sem("rope_done")
        relu_done = sem("relu_done")
        dve_step = sem("dve_step")
        kv_hi_done = sem("kv_hi_done")
        staged = sem("staged")
        stored = sems("stored", 2)
        prob_done = sem("prob_done")
        pv_done = sem("pv_done")
        sink_sum = sem("sink_sum")
        sink_done = sem("sink_done")
        hi_done = sem("hi_done")
        x_res_in = sems("x_res_in", 2)
        gb_in = sem("gb_in")
        bn_done = sem("bn_done")
        std_done = sem("std_done")
        ln_done = sem("ln_done")
        mem_bias_done = sem("mem_bias_done")
        mem_prob_done = sem("mem_prob_done")
        sq_done = sem("sq_done")
        hid_hi_done = sem("hid_hi_done")
        hid_ready = sem("hid_ready")
        out_done = sem("out_done")

        qk_dram = nc.dram_tensor("qk_dram", [2, 14 * P, SEQ], F32, kind="Internal").ap()
        g_dram = nc.dram_tensor("g_dram", [NK, P, D], F32, kind="Internal").ap()
        u_dram = nc.dram_tensor("u_dram", [NK, P, D], F32, kind="Internal").ap()

        CONSTS = [("ident", ident), ("rot", rot), ("swa_mask", swa_mask), ("causal", causal),
                  ("bias_qk", bias_qk)]
        N_CONSTS = len(CONSTS) + 2

        def slot_of(c):
            return c % 2 if c < C_MIX else (c - C_MIX) % 4

        def columns_of(c):
            return NK * V_COLS if c == C_V else CHUNK

        def source_of(c):
            if c < C_MEM:
                return [a["w_v"], a["w_k"], a["w_iq"][0], a["w_iq"][1], a["w_dq"][0], a["w_dq"][1],
                        a["w_sq"][0], a["w_sq"][1]][c]
            if c < C_MIX:
                h, what = divmod(c - C_MEM, 4)
                return a[("wk_mem", "wv_mem", "wq_mem", "wo_mem")[what]][h]
            if c < C_G:
                return a["w_o"][c - C_MIX]
            if c < C_MLP:
                dram = g_dram if c < C_U else u_dram
                ch, kh = divmod((c - C_G) % 4, 2)
                return dram[4 * kh:4 * kh + 4, :, ch * HALF:(ch + 1) * HALF].rearrange("k p n -> p k n")
            f, what = divmod(c - C_MLP, 2)
            return a[("w_up", "w_down")[what]][f]

        block = ctx.enter_context(nc.Block())

        @block.sync
        def _(sp):
            def load_gb(n):
                sp.dma_start(gamma[:], a["gamma"][n].partition_broadcast(P)).then_inc(gb_in, 16)
                sp.dma_start(beta[:], a["beta"][n].partition_broadcast(P)).then_inc(gb_in, 16)

            def load_queries(j):
                if j < NT - FIRST_TOPK_TILE:
                    row, i = HEAD_ROW["iq"], FIRST_TOPK_TILE + j
                    units = N_ROPE_FIRST
                else:
                    kind, i, _ = ATT[(j - (NT - FIRST_TOPK_TILE)) * HEADS]
                    row = HEAD_ROW[kind]
                    units = len(ROPE)
                for s in range(2):
                    sp.wait_ge(qk_stored[s], 32 * (units // 2))
                if j >= 3:
                    filled(sp, l_full, (j - 3) * HEADS + HEADS - 1)
                for part in range(2):
                    sp.dma_start(q_tile[j % 3][part * HEAD:(part + 1) * HEAD, :, :].bitcast(F32),
                                 qk_dram[part, row:row + HEADS * HEAD, i * P:(i + 1) * P]
                                 .rearrange("(h d) t -> d h t", d=HEAD)).then_inc(q_in[j % 3], 16)

            def load_keys():
                for s in range(2):
                    sp.wait_ge(qk_stored[s], 32 * 2)
                for j in range(4):
                    for part, key in enumerate((key_hi[j], key_lo[j])):
                        for half in range(2):
                            sp.dma_start(key[half * HEAD:(half + 1) * HEAD, :].bitcast(F32),
                                         qk_dram[part, j * HEAD:(j + 1) * HEAD, :]).then_inc(keys_in, 16)

            sp.dma_start(pos_i[:], a["positions"].partition_broadcast(P)).then_inc(pos_in, 16)
            sp.dma_start(inv_freq[:], a["inv_freq"]).then_inc(pos_in, 16)
            sp.dma_start(raw[0][:, 0:columns_of(0)], source_of(0)).then_inc(raw_in[0], 16)
            for k in range(NK):
                sp.dma_start(x_raw[k][:], a["x_t"][k]).then_inc(x_in[k], 16)
            sp.dma_start(b_v[:], a["bias_v"].partition_broadcast(P)).then_inc(consts_in, 16)
            sp.dma_start(sinks[:], a["sinks"].partition_broadcast(P)).then_inc(consts_in, 16)
            for name, tile in CONSTS:
                sp.dma_start(tile[:], a[name]).then_inc(consts_in, 16)
            sp.dma_start(raw[1][:], source_of(1)).then_inc(raw_in[1], 16)
            for c in range(2, N_CHUNKS):
                if c == C_SQ:
                    load_keys()
                    for j in range(NT - FIRST_TOPK_TILE):
                        load_queries(j)
                if c == C_MEM:
                    chunk_used(sp, C_MEM - 1)
                    sp.dma_start(mem_raw[:], a["mem_t"]).then_inc(mem_in, 16)
                    for j in range(3):
                        load_queries(NT - FIRST_TOPK_TILE + j)
                if c == C_MIX + 2:
                    for j in range(3, 2 * NT):
                        load_queries(NT - FIRST_TOPK_TILE + j)
                if c == C_MIX + 2:
                    chunk_used(sp, C_MIX - 1)
                    for s in range(2):
                        sp.wait_ge(stored[s], 16 * 4 * MEM_HEADS)
                    filled(sp, a_full, A_ATT + 2 * NT - 1)
                    load_gb(0)
                if c == C_U + 1:
                    sp.wait_ge(ln_done, NT)
                    load_gb(1)
                if c == C_MLP + 2:
                    sp.wait_ge(ln_done, 2 * NT)
                    load_gb(2)
                sp.wait_ge(w_ready, c - 1)
                dst = raw[c % 2][:, 0:columns_of(c)]
                if C_G <= c < C_MLP:
                    dst = dst.rearrange("p (k n) -> p k n", k=4)
                sp.dma_start(dst, source_of(c)).then_inc(raw_in[c % 2], 16)
            for t in range(NT):
                sp.wait_ge(ln_done, 2 * NT + t + 1)
                sp.dma_start(a["out"][t], h_buf[:, t, :]).then_inc(out_done, 16)
            sp.wait_ge(out_done, 16 * NT)

        @block.gpsimd
        def _(pool):
            for c in range(N_CHUNKS):
                s, n = slot_of(c), columns_of(c)
                pool.wait_ge(raw_in[c % 2], 16 * (c // 2 + 1))
                if 2 <= c < C_MIX + 2:
                    chunk_used(pool, c - 2)
                elif C_MIX + 2 <= c < C_MIX + 4:
                    filled(pool, a_full, A_ATT + 2 * NT - 1)
                elif c >= C_MIX + 4:
                    chunk_used(pool, c - 4)
                pool.tensor_scalar(w_hi[s][:, 0:n], raw[c % 2][:, 0:n], 1.0, 1.0, ALU.mult, ALU.mult)\
                    .then_inc(w_rounded, 1)
                pool.wait_ge(w_rounded, c + 1)
                pool.tensor_tensor(w_lo[s][:, 0:n], raw[c % 2][:, 0:n], w_hi[s][:, 0:n].bitcast(F32),
                                   ALU.subtract).then_inc(w_ready, 1)

        @block.tensor
        def _(pe):
            def exact(dst, parts, first=True, final=True):
                for n, (lh, ll, rh, rl) in enumerate(parts):
                    pe.matmul(dst, lh, rh, start=(first and n == 0), stop=False)
                    pe.matmul(dst, lh, rl, start=False, stop=False)
                    last = pe.matmul(dst, ll, rh, start=False, stop=(final and n == len(parts) - 1))
                return last

            def parts_of(c, k):
                s, n = slot_of(c), columns_of(c)
                return [w[s][:, 0:n].rearrange("p (k n) -> p k n", k=k) for w in (w_hi, w_lo)]

            pe.wait_ge(w_ready, C_V + 1)
            wh, wl = parts_of(C_V, NK)
            for k in range(NK):
                pe.wait_ge(x_lo_done, k + 1)
                for t in range(NT):
                    tok = slice(t * P, (t + 1) * P)
                    mm = exact(v_bank[t][:, 0:V_COLS], [(x_hi[:, k, tok], x_lo[:, k, tok], wh[:, k, :], wl[:, k, :])],
                               first=(k == 0), final=(k == NK - 1))
                    if k == NK - 1:
                        mm.then_inc(v_full, 1)

            def project(r):
                c, j, _, hf = ROPE[r]
                n = A_ROPE + r
                if r == 0:
                    pe.wait_ge(v_done, 2)
                pe.wait_ge(w_ready, c + 1)
                freed(pe, a_free, n)
                wh, wl = parts_of(c, NK)
                col = slice(j * P, (j + 1) * P)
                tok = slice(hf * HALF, (hf + 1) * HALF)
                exact(ring_a[n % 2][:], [(wh[:, k, col], wl[:, k, col], x_hi[:, k, tok], x_lo[:, k, tok])
                                         for k in range(NK)]).then_inc(a_full[n % 2], 1)

            def rotate(r):
                n = T_ROT + r
                if r == 0:
                    pe.wait_ge(v_done, NT)
                pe.wait_ge(consts_in, 16 * N_CONSTS)
                emptied(pe, a_free, A_ROPE + r)
                freed(pe, t_free, n)
                pe.matmul(ring_t[n % 2][:], rot[:], q_raw[r % 2][:], start=True, stop=True)\
                    .then_inc(t_full[n % 2], 1)

            def project_and_rotate(r0, r1):
                for r in range(r0, r1 + 1):
                    if r < r1:
                        project(r)
                    if r > r0:
                        rotate(r - 1)

            def split_scores(dst, q, key, k0, width):
                for lo in range(0, width, HALF):
                    hi = min(lo + HALF, width)
                    pe.matmul(dst[:, lo:hi], q, key_hi[key][:, k0 + lo:k0 + hi], start=True, stop=False)
                    mm = pe.matmul(dst[:, lo:hi], q, key_lo[key][:, k0 + lo:k0 + hi], start=False, stop=True)
                return mm

            def index_scores(n):
                i, h = IDX[n]
                j = n // HEADS
                pe.wait_ge(keys_in, 16 * 16)
                pe.wait_ge(q_in[j % 3], 32 * (j // 3 + 1))
                freed(pe, l_free, L_IDX + n)
                split_scores(ring_l[n % 2], q_tile[j % 3][:, h, :], 1, 0, (i + 1) * P)\
                    .then_inc(l_full[n % 2], 1)

            def memory_head(h):
                n = A_MEM + 10 * h
                for kv in range(2):
                    pe.wait_ge(w_ready, C_MEM + 4 * h + kv + 1)
                    freed(pe, a_free, n + kv)
                    wh, wl = parts_of(C_MEM + 4 * h + kv, NK)
                    for j in range(2):
                        col = slice(j * P, (j + 1) * P)
                        mm = exact(ring_a[(n + kv) % 2][:, j * MEM:(j + 1) * MEM],
                                   [(wh[:, k, col], wl[:, k, col], mem_hi[:, k, :], mem_lo[:, k, :])
                                    for k in range(NK)])
                    mm.then_inc(a_full[(n + kv) % 2], 1)
                for use in range(4):
                    m = n + 2 + use
                    pe.wait_ge(w_ready, C_MEM + 4 * h + 3)
                    emptied(pe, a_free, n)
                    freed(pe, a_free, m)
                    wh, wl = parts_of(C_MEM + 4 * h + 2, 2)
                    for j in range(2):
                        col = slice((2 * use + j) * P, (2 * use + j + 1) * P)
                        mm = exact(ring_a[m % 2][:, j * MEM:(j + 1) * MEM],
                                   [(wh[:, k, col], wl[:, k, col], kv_hi[0][:, k, :], kv_lo[0][:, k, :])
                                    for k in range(2)])
                    mm.then_inc(a_full[m % 2], 1)
                for use in range(4):
                    m = n + 6 + use
                    mt, half = divmod(use, 2)
                    pe.wait_ge(w_ready, C_MEM + 4 * h + 4)
                    emptied(pe, a_free, n + 1)
                    freed(pe, a_free, m)
                    wh, wl = parts_of(C_MEM + 4 * h + 3, 2)
                    row = slice(mt * P, (mt + 1) * P)
                    col = slice(half * HALF, (half + 1) * HALF)
                    exact(ring_a[m % 2][:], [(kv_hi[1][:, k, row], kv_lo[1][:, k, row],
                                              wh[:, k, col], wl[:, k, col]) for k in range(2)])\
                        .then_inc(a_full[m % 2], 1)

            def scores(n):
                kind, i, h = ATT[n]
                k0, nk = keys_of(ATT[n])
                key = 0 if kind == "D" else 2 + h // (HEADS // 2)
                j = NT - FIRST_TOPK_TILE + n // HEADS
                pe.wait_ge(q_in[j % 3], 32 * (j // 3 + 1))
                freed(pe, l_free, L_ATT + n)
                m = L_ATT + n
                split_scores(ring_l[m % 2], q_tile[j % 3][:, h, :], key, k0 * P, nk * P)\
                    .then_inc(l_full[m % 2], 1)

            def turn_probs(n):
                nk = keys_of(ATT[n])[1]
                pe.wait_ge(prob_done, n + 1)
                for g in range((nk + 3) // 4):
                    m = T_ATT[n] + g
                    freed(pe, t_free, m)
                    for j in range(4 * g, min(4 * g + 4, nk)):
                        mm = pe.transpose(ring_t[m % 2][:, (j % 4) * P:(j % 4 + 1) * P],
                                          prob[n % 2][:, j * P:(j + 1) * P], ident[:])
                    mm.then_inc(t_full[m % 2], 1)

            def times_values(n):
                kind, i, h = ATT[n]
                k0, nk = keys_of(ATT[n])
                m = A_ATT + n // HEADS
                if h == 0:
                    freed(pe, a_free, m)
                for g in range((nk + 3) // 4):
                    emptied(pe, t_free, T_ATT[n] + g)
                v0 = HEADS if kind == "D" else HEADS + HEAD + HEAD * (h // (HEADS // 2))
                for j in range(nk):
                    mm = pe.matmul(ring_a[m % 2][:, h * HEAD:(h + 1) * HEAD],
                                   prob_t[n % 2][:, j * P:(j + 1) * P],
                                   v_all[:, k0 + j, v0:v0 + HEAD], start=(j == 0), stop=(j == nk - 1))
                mm.then_inc(a_full[m % 2] if h == HEADS - 1 else pv_done, 1)

            def turn_tile(n, block_of):
                for g in range(2):
                    freed(pe, t_free, n + g)
                    for j in range(4):
                        mm = pe.transpose(ring_t[(n + g) % 2][:, j * P:(j + 1) * P],
                                          block_of(4 * g + j), ident[:])
                    mm.then_inc(t_full[(n + g) % 2], 1)

            def turn_o(t):
                emptied(pe, a_free, A_ATT + t)
                emptied(pe, a_free, A_ATT + NT + t)
                turn_tile(T_O + 2 * t, lambda k: h_buf[:, t, k * P:(k + 1) * P])

            def turn_result(stage, t):
                n = T_STAGE + 2 * (stage * NT + t)
                if stage == 1:
                    pe.wait_ge(mem_prob_done, NT + t + 1)
                    turn_tile(n, lambda k: p_store[:, t, k * P:(k + 1) * P] if k < 4
                              else p_work[t % 2][:, (k - 4) * P:(k - 3) * P])
                else:
                    pe.wait_ge(ln_done, (stage // 2) * NT + t + 1)
                    turn_tile(n, lambda k: h_buf[:, t, k * P:(k + 1) * P])

            def act_split(stage, t):
                n = T_O + 2 * t if stage == 0 else T_STAGE + 2 * ((stage - 1) * NT + t)
                emptied(pe, t_free, n)
                emptied(pe, t_free, n + 1)

            def product(g):
                stage, ch, t = g // (2 * NT), g // NT % 2, g % NT
                n = L_GEMM + g
                c = C_MIX + 4 * stage + 2 * ch
                pe.wait_ge(w_ready, c + 2)
                act_split(stage, t)
                freed(pe, l_free, n)
                for kh in range(2):
                    wh, wl = parts_of(c + kh, 4)
                    mm = exact(ring_l[n % 2][:, 0:HALF],
                               [(act_hi[:, t, 4 * kh + k, :], act_lo[:, t, 4 * kh + k, :],
                                 wh[:, k, :], wl[:, k, :]) for k in range(4)],
                               first=(kh == 0), final=(kh == 1))
                mm.then_inc(l_full[n % 2], 1)

            def up(u):
                f, hf = divmod(u, 2)
                wh, wl = parts_of(C_MLP + 2 * f, NK)
                pe.wait_ge(w_ready, C_MLP + 2 * f + 1)
                if f == 0:
                    for t in range(4 * hf, 4 * hf + 4):
                        act_split(3, t)
                for j in range(2):
                    n = A_UP + 2 * u + j
                    freed(pe, a_free, n)
                    col = slice(j * P, (j + 1) * P)
                    tiles = slice(4 * hf, 4 * hf + 4)
                    exact(ring_a[n % 2][:], [(wh[:, k, col], wl[:, k, col],
                                              act_hi[:, tiles, k, :], act_lo[:, tiles, k, :])
                                             for k in range(NK)]).then_inc(a_full[n % 2], 1)

            def down(u):
                f = u // 2
                wh, wl = parts_of(C_MLP + 2 * f + 1, 2)
                pe.wait_ge(w_ready, C_MLP + 2 * f + 2)
                pe.wait_ge(hid_ready, 2 * u + 2)
                for tt in range(4):
                    n = L_DOWN + 4 * u + tt
                    freed(pe, l_free, n)
                    tok = slice(tt * P, (tt + 1) * P)
                    for half in range(2):
                        col = slice(half * HALF, (half + 1) * HALF)
                        mm = exact(ring_l[n % 2][:, col],
                                   [(hid_hi[u % 2][:, j, tok], hid_lo[u % 2][:, j, tok],
                                     wh[:, j, col], wl[:, j, col]) for j in range(2)])
                    mm.then_inc(l_full[n % 2], 1)

            project_and_rotate(0, N_ROPE_FIRST)
            for n in range(len(IDX)):
                index_scores(n)
            project_and_rotate(N_ROPE_FIRST, len(ROPE))
            pe.wait_ge(mem_lo_done, 1)
            for h in range(MEM_HEADS):
                memory_head(h)
            for n in range(len(ATT) + 3):
                if n < len(ATT):
                    scores(n)
                if 0 <= n - 2 < len(ATT):
                    turn_probs(n - 2)
                if 0 <= n - 3 < len(ATT):
                    times_values(n - 3)
            turn_o(0)
            turn_o(1)
            for g in range(N_GEMM):
                product(g)
                if g + 2 < NT:
                    turn_o(g + 2)
                if transposed_at(g):
                    turn_result(*transposed_at(g))
            up(0)
            for g in (N_GEMM, N_GEMM + 1):
                turn_result(*transposed_at(g))
            for u in range(2 * N_FF):
                if u + 1 < 2 * N_FF:
                    up(u + 1)
                down(u)

        @block.scalar
        def _(act):
            for k in range(NK):
                act.wait_ge(x_in[k], 16)
                act.activation(x_hi[:, k, :], x_raw[k][:], ACT.Copy).then_inc(x_hi_done, 1)
                if k == 1:
                    act.wait_ge(trig_steps, 1)
                    act.activation(sin[:], angle[:], ACT.Sin).then_inc(trig_done, 1)
                    act.wait_ge(trig_steps, 2)
                    act.activation(cos[:], turns[:], ACT.Sin).then_inc(trig_done, 1)
            act.wait_ge(consts_in, 16 * N_CONSTS)

            def add_bias(r):
                n = A_ROPE + r
                filled(act, a_full, n)
                if r >= 2:
                    act.wait_ge(rope_done, r - 1)
                b = BIAS_COLUMN[ROPE[r][2]]
                act.activation(q_raw[r % 2][:], ring_a[n % 2][:], ACT.Identity,
                               bias=bias_qk[:, b:b + 1]).then_inc(a_free[n % 2], 1)

            def round_roped(r):
                act.wait_ge(rope_done, r + 1)
                if r >= 2:
                    act.wait_ge(qk_stored[r % 2], 32 * (r // 2))
                act.activation(q_hi[r % 2][:], roped[r % 2][:], ACT.Copy).then_inc(q_rounded, 1)

            def store_roped(r):
                _, _, what, hf = ROPE[r]
                row = BIAS_COLUMN[what] * P
                tok = slice(hf * HALF, (hf + 1) * HALF)
                act.wait_ge(q_rounded, r + 1)
                act.wait_ge(q_split, r + 1)
                act.dma_start(qk_dram[0, row:row + P, tok], q_hi[r % 2][:].bitcast(F32)).then_inc(qk_stored[r % 2], 16)
                act.dma_start(qk_dram[1, row:row + P, tok], roped[r % 2][:])\
                    .then_inc(qk_stored[r % 2], 16)

            def evacuate(r0, r1):
                for r in range(r0, r1 + 2):
                    if r < r1:
                        add_bias(r)
                    if r0 <= r - 1 < r1:
                        round_roped(r - 1)
                    if r0 <= r - 2:
                        store_roped(r - 2)

            evacuate(0, N_ROPE_FIRST)
            for n in range(len(IDX)):
                width = (IDX[n][0] + 1) * P
                filled(act, l_full, L_IDX + n)
                act.activation(ring_l[n % 2][:, 0:width], ring_l[n % 2][:, 0:width], ACT.Relu)\
                    .then_inc(relu_done, 1)
            evacuate(N_ROPE_FIRST, len(ROPE))

            act.wait_ge(mem_in, 16)
            act.activation(mem_hi[:], mem_raw[:], ACT.Copy).then_inc(mem_hi_done, 1)
            act.wait_ge(rope_done, len(ROPE))
            for s in range(2):
                act.wait_ge(qk_stored[s], 16 * len(ROPE))
            for h in range(MEM_HEADS):
                n = A_MEM + 10 * h
                for kv in range(2):
                    filled(act, a_full, n + kv)
                    act.activation(kv_hi[kv][:], ring_a[(n + kv) % 2][:], ACT.Copy).then_inc(kv_hi_done, 1)
                for use in range(8):
                    m = n + 2 + use
                    e = 8 * h + use
                    filled(act, a_full, m)
                    if e >= 2:
                        act.wait_ge(stored[e % 2], 16 * (e // 2))
                    act.activation(stage_out[e % 2][:], ring_a[m % 2][:], ACT.Copy).then_inc(a_free[m % 2], 1)
                    emptied(act, a_free, m)
                    if use < 4:
                        dst = g_dram[2 * use:2 * use + 2, :, h * MEM:(h + 1) * MEM].rearrange("k p n -> p k n")
                        src = stage_out[e % 2][:].rearrange("p (k n) -> p k n", k=2)
                    else:
                        mt, half = divmod(use - 4, 2)
                        dst = u_dram[2 * h + mt, :, half * HALF:(half + 1) * HALF]
                        src = stage_out[e % 2][:]
                    act.dma_start(dst, src).then_inc(stored[e % 2], 16)

            def exp_unit(n):
                width = keys_of(ATT[n])[1] * P
                emptied(act, l_free, L_ATT + n)
                if n >= 2:
                    filled(act, t_full, T_ATT[n - 1] - 1)
                act.activation(prob[n % 2][:, 0:width], logit[n % 2][:, 0:width], ACT.Exp, scale=-1.0,
                               bias=neg_max[:, n:n + 1], accum_out=sums[:, n:n + 1]).then_inc(prob_done, 1)

            def move_probs(n):
                nk = keys_of(ATT[n])[1]
                if n >= 2:
                    multiplied(act, n - 2)
                for g in range((nk + 3) // 4):
                    m = T_ATT[n] + g
                    filled(act, t_full, m)
                    w = min(4, nk - 4 * g) * P
                    act.activation(prob_t[n % 2][:, g * HALF:g * HALF + w], ring_t[m % 2][:, 0:w],
                                   ACT.Copy).then_inc(t_free[m % 2], 1)

            def exp_sinks(tile):
                act.wait_ge(sink_sum, tile + 1)
                act.activation(sink_exp[:], sink_exp[:], ACT.Exp).then_inc(sink_done, 1)

            for n in range(len(ATT) + 2):
                if 0 <= n - 1 < len(ATT):
                    exp_unit(n - 1)
                if 0 <= n - 2:
                    move_probs(n - 2)
                last = n - 3
                if last % HEADS == HEADS - 1 and 0 <= last and ATT[last][0] == "S":
                    exp_sinks(last // HEADS)

            def round_groups(n, t):
                for g in range(2):
                    filled(act, t_full, n + g)
                    act.activation(act_hi[:, t, 4 * g:4 * g + 4, :], ring_t[(n + g) % 2][:], ACT.Copy)\
                        .then_inc(hi_done, 1)

            def load_x(g):
                ch, t = divmod(g, NT)
                if g >= 2:
                    emptied(act, l_free, L_GEMM + g - 2)
                act.dma_start(x_res[g % 2][:], a["x"][t][:, ch * HALF:(ch + 1) * HALF])\
                    .then_inc(x_res_in[g % 2], 16)

            def root(n):
                act.wait_ge(bn_done, n + 1)
                act.activation(std[n % 2][:], mean_var[n % 2][:, 1:2], ACT.Sqrt, bias=eps[:])\
                    .then_inc(std_done, 1)

            emptied(act, a_free, A_ATT + 2 * NT - 1)
            load_x(0)
            load_x(1)
            round_groups(T_O, 0)
            round_groups(T_O + 2, 1)
            for g in range(N_GEMM):
                stage, ch, t = g // (2 * NT), g // NT % 2, g % NT
                if stage == 1:
                    dst = p_store[:, t, :] if ch == 0 else p_work[t % 2][:]
                    act.wait_ge(mem_bias_done, g - 2 * NT + 1)
                    if ch == 1 and t >= 2:
                        filled(act, t_full, T_STAGE + 2 * (NT + t - 2) + 1)
                    n = L_GEMM + g
                    for hh in range(2):
                        col = slice(hh * MEM, (hh + 1) * MEM)
                        e = act.activation(dst[:, col], ring_l[n % 2][:, col], ACT.Exp, scale=MEM_SCALE,
                                           bias=mem_bias[g % 2][:, hh:hh + 1],
                                           accum_out=mem_sum[g % 2][:, hh:hh + 1])
                    e.then_inc(l_free[n % 2], 1)
                if g + 2 < NT:
                    round_groups(T_O + 2 * (g + 2), g + 2)
                if stage == 0 and g + 2 < 2 * NT:
                    load_x(g + 2)
                if stage != 1 and ch == 1:
                    root(stage // 2 * NT + t)
                if transposed_at(g):
                    s, tt = transposed_at(g)
                    round_groups(T_STAGE + 2 * (s * NT + tt), tt)

            def rectify(u):
                for j in range(2):
                    q = 2 * u + j
                    filled(act, a_full, A_UP + q)
                    if q >= 2:
                        act.wait_ge(hid_ready, q - 1)
                    act.activation(relu_buf[q % 2][:], ring_a[(A_UP + q) % 2][:], ACT.Relu)\
                        .then_inc(a_free[(A_UP + q) % 2], 1)

            def round_hidden(u):
                for j in range(2):
                    q = 2 * u + j
                    act.wait_ge(sq_done, q + 1)
                    act.activation(hid_hi[u % 2][:, j, :], relu_buf[q % 2][:], ACT.Copy)\
                        .then_inc(hid_hi_done, 1)

            rectify(0)
            for g in (N_GEMM, N_GEMM + 1):
                s, tt = transposed_at(g)
                round_groups(T_STAGE + 2 * (s * NT + tt), tt)
            round_hidden(0)
            for u in range(2 * N_FF):
                if u + 1 < 2 * N_FF:
                    rectify(u + 1)
                    round_hidden(u + 1)
                if u >= 2 * N_FF - 2:
                    for tt in range(4):
                        root(2 * NT + 4 * (u % 2) + tt)

        @block.vector
        def _(dve):
            steps = [0]

            def chain(ins):
                steps[0] += 1
                ins.then_inc(dve_step, 1)
                dve.wait_ge(dve_step, steps[0])

            def then(ins):
                steps[0] += 1
                ins.then_inc(dve_step, 1)
                return steps[0]

            dve.wait_ge(pos_in, 32)
            chain(dve.tensor_copy(turns[:], pos_i[:]))
            chain(dve.tensor_scalar(angle[:], turns[:], inv_freq[:], None, ALU.mult))
            chain(dve.tensor_scalar(turns[:], angle[:], 1.0 / TWO_PI, ROUND, ALU.mult, ALU.add))
            chain(dve.tensor_scalar(turns[:], turns[:], -ROUND, None, ALU.add))
            for part in (PI_A, PI_B, PI_C):
                chain(dve.scalar_tensor_tensor(out=angle[:], in0=turns[:], scalar=-part, in1=angle[:],
                                               op0=ALU.mult, op1=ALU.add))
            dve.tensor_scalar(angle[:], angle[:], PI_DOWN, -PI_DOWN, ALU.min, ALU.max).then_inc(trig_steps, 1)
            dve.wait_ge(trig_steps, 1)
            chain(dve.tensor_scalar(turns[:], angle[:], -1.0, None, ALU.mult))
            chain(dve.tensor_tensor(turns[:], turns[:], angle[:], ALU.min))
            dve.tensor_scalar(turns[:], turns[:], float(np.pi / 2), None, ALU.add).then_inc(trig_steps, 1)
            chain(dve.memset(eps[:], LN_EPS))
            for k in range(NK):
                dve.wait_ge(x_hi_done, k + 1)
                dve.tensor_tensor(x_lo[:, k, :], x_raw[k][:], x_hi[:, k, :].bitcast(F32), ALU.subtract)\
                    .then_inc(x_lo_done, 1)
            dve.wait_ge(x_lo_done, NK)
            dve.wait_ge(consts_in, 16 * N_CONSTS)
            for t in range(NT):
                dve.wait_ge(v_full, t + 1)
                dve.tensor_tensor(v_all[:, t, :], v_bank[t][:, 0:V_COLS], b_v[:], ALU.add).then_inc(v_done, 1)
            chain(dve.tensor_scalar(neg_sinks[:], sinks[:], -1.0, None, ALU.mult))

            def rope(r):
                hf = ROPE[r][3]
                n = T_ROT + r
                tok = slice(hf * HALF, (hf + 1) * HALF)
                if r == 0:
                    dve.wait_ge(trig_done, 2)
                else:
                    dve.wait_ge(rope_done, r)
                if r >= 2:
                    dve.wait_ge(qk_stored[r % 2], 32 * (r // 2))
                emptied(dve, a_free, A_ROPE + r)
                c1 = then(dve.tensor_tensor(roped[r % 2][:], q_raw[r % 2][:], cos[:, tok], ALU.mult))
                filled(dve, t_full, n)
                dve.tensor_tensor(rot_part[:], ring_t[n % 2][:], sin[:, tok], ALU.mult)\
                    .then_inc(t_free[n % 2], 1)
                dve.wait_ge(dve_step, c1)
                emptied(dve, t_free, n)
                dve.tensor_tensor(roped[r % 2][:], roped[r % 2][:], rot_part[:], ALU.add).then_inc(rope_done, 1)

            def split_roped(r):
                dve.wait_ge(q_rounded, r + 1)
                dve.tensor_tensor(roped[r % 2][:].bitcast(F32R), roped[r % 2][:], q_hi[r % 2][:].bitcast(F32), ALU.subtract)\
                    .then_inc(q_split, 1)

            def rotate_and_split(r0, r1, us):
                for r in range(r0, r1 + 1):
                    if r < r1:
                        rope(r)
                    if r > r0:
                        split_roped(r - 1)
                    if us:
                        select_for(us)

            def index_sum(n):
                i, h = IDX[n]
                width = (i + 1) * P
                dve.wait_ge(relu_done, n + 1)
                src, w = ring_l[n % 2][:, 0:width], v_all[:, i, h:h + 1]
                if h == 0:
                    dve.wait_ge(v_done, NT)
                    dve.tensor_scalar(score[i][:], src, w, None, ALU.mult).then_inc(l_free[n % 2], 1)
                else:
                    emptied(dve, l_free, n - 1)
                    dve.scalar_tensor_tensor(out=score[i][:], in0=src, scalar=w, in1=score[i][:],
                                             op0=ALU.mult, op1=ALU.add).then_inc(l_free[n % 2], 1)
                if h == HEADS - 1:
                    emptied(dve, l_free, n)
                    chain(dve.tensor_scalar(score[i][:], score[i][:], IDX_SCALE, None, ALU.mult))
                    own = slice(i * P, width)
                    chain(dve.tensor_tensor(score[i][:, own], score[i][:, own], causal[:, P:2 * P], ALU.add))

            def select_keys():
                for pair in ((2, 3), (4, 5), (6, 7)):
                    cost = sum(2 * (0.07 + (i + 1) * P / 960.0) for i in pair)
                    taken = [0, 0]
                    for _ in range(TOPK // 8):
                        top = [0, 0]
                        for s, i in enumerate(pair):
                            dve.wait_ge(dve_step, max(taken[s], 1))
                            top[s] = then(dve.max(m8[s][:], score[i][:]))
                        for s, i in enumerate(pair):
                            dve.wait_ge(dve_step, top[s])
                            taken[s] = then(dve.match_replace(score[i][:], m8[s][:], score[i][:], TAKEN))
                        yield cost, None
                    for s, i in enumerate(pair):
                        dve.wait_ge(dve_step, taken[s])
                        chain(dve.tensor_scalar(score[i][:], score[i][:], TAKEN / 2, MASKED,
                                                ALU.is_gt, ALU.mult))
                        yield 0.6, i

            selection = select_keys()
            selected = set(range(FIRST_TOPK_TILE))

            def select_for(us):
                while us > 0:
                    cost, tile = next(selection, (1e9, None))
                    us -= cost
                    if tile is not None:
                        selected.add(tile)

            def select_until(i):
                while i not in selected:
                    selected.add(next(selection)[1])

            rotate_and_split(0, N_ROPE_FIRST, 0)
            for n in range(len(IDX)):
                index_sum(n)
            rotate_and_split(N_ROPE_FIRST, len(ROPE), 3.0)

            dve.wait_ge(mem_hi_done, 1)
            dve.tensor_tensor(mem_lo[:], mem_raw[:], mem_hi[:].bitcast(F32), ALU.subtract)\
                .then_inc(mem_lo_done, 1)
            for h in range(MEM_HEADS):
                for kv in range(2):
                    n = A_MEM + 10 * h + kv
                    dve.wait_ge(kv_hi_done, 2 * h + kv + 1)
                    dve.tensor_tensor(kv_lo[kv][:], ring_a[n % 2][:], kv_hi[kv][:].bitcast(F32),
                                      ALU.subtract).then_inc(a_free[n % 2], 1)
                    select_for(3 if kv == 0 else 20)

            def mask_logits(n):
                kind, i, h = ATT[n]
                if kind == "D":
                    select_until(i)
                width = keys_of(ATT[n])[1] * P
                if kind == "S":
                    mask = swa_mask[:, 2 * P - width:]
                    start = neg_sinks[:, h:h + 1]
                else:
                    mask = causal[:, 2 * P - width:] if i < FIRST_TOPK_TILE else score[i][:]
                    start = 3.0e38
                m = L_ATT + n
                filled(dve, l_full, m)
                if n >= 2:
                    dve.wait_ge(prob_done, n - 1)
                dve.tensor_tensor_reduce(logit[n % 2][:, 0:width], ring_l[m % 2][:, 0:width], mask,
                                         -SCALE, start, ALU.add, ALU.min, neg_max[:, n:n + 1])\
                    .then_inc(l_free[m % 2], 1)

            def add_sinks(tile):
                emptied(dve, l_free, L_ATT + tile * HEADS + HEADS - 1)
                if tile:
                    emptied(dve, a_free, A_ATT + tile - 1)
                dve.tensor_tensor(sink_exp[:], neg_max[:, tile * HEADS:(tile + 1) * HEADS], sinks[:],
                                  ALU.add).then_inc(sink_sum, 1)

            def normalise(tile):
                m = A_ATT + tile
                total = sums[:, tile * HEADS:(tile + 1) * HEADS]
                dve.wait_ge(prob_done, (tile + 1) * HEADS)
                if tile:
                    emptied(dve, a_free, m - 1)
                if tile < NT:
                    dve.wait_ge(sink_done, tile + 1)
                    chain(dve.tensor_tensor(total, total, sink_exp[:], ALU.add))
                chain(dve.reciprocal(inv_sum[:], total))
                filled(dve, a_full, m)
                col = HEADS * HEAD if tile < NT else 0
                dve.tensor_tensor(h_buf[:, tile % NT, col:col + HEADS * HEAD]
                                  .rearrange("p (h d) -> p h d", h=HEADS),
                                  ring_a[m % 2][:].rearrange("p (h d) -> p h d", h=HEADS),
                                  inv_sum[:].rearrange("p (h o) -> p h o", o=1)
                                  .to_broadcast([P, HEADS, HEAD]), ALU.mult).then_inc(a_free[m % 2], 1)

            for n in range(len(ATT) + 4):
                if n < len(ATT):
                    mask_logits(n)
                last = n - 2
                if last >= 0 and last % HEADS == HEADS - 1 and last < NT * HEADS:
                    add_sinks(last // HEADS)
                last = n - 4
                if last >= 0 and last % HEADS == HEADS - 1:
                    normalise(last // HEADS)
                if n < NT * HEADS:
                    select_for(1.0)

            def low_groups(n, t, count):
                for g in range(2):
                    dve.wait_ge(hi_done, count + g + 1)
                    dve.tensor_tensor(act_lo[:, t, 4 * g:4 * g + 4, :], ring_t[(n + g) % 2][:],
                                      act_hi[:, t, 4 * g:4 * g + 4, :].bitcast(F32), ALU.subtract)\
                        .then_inc(t_free[(n + g) % 2], 1)

            def moments(n, t):
                for half in range(2):
                    c = then(dve.bn_stats(bn[n % 2][:, half, :], h_buf[:, t, half * HALF:(half + 1) * HALF]))
                dve.wait_ge(dve_step, c)
                dve.bn_aggr(mean_var[n % 2][:], bn[n % 2][:]).then_inc(bn_done, 1)

            def norm(n, t):
                dve.wait_ge(bn_done, n + 1)
                if n:
                    dve.wait_ge(ln_done, n)
                c1 = then(dve.tensor_scalar(var_eps[:], mean_var[n % 2][:, 1:2], LN_EPS, None, ALU.add))
                dve.wait_ge(gb_in, 32 * (n // NT + 1))
                dve.wait_ge(std_done, n + 1)
                c2 = then(dve.reciprocal(rstd0[:], std[n % 2][:]))
                c3 = then(dve.scalar_tensor_tensor(out=h_buf[:, t, :], in0=h_buf[:, t, :],
                                                   scalar=mean_var[n % 2][:, 0:1], in1=gamma[:],
                                                   op0=ALU.subtract, op1=ALU.mult))
                dve.wait_ge(dve_step, max(c1, c2))
                chain(dve.scalar_tensor_tensor(out=newton[:], in0=rstd0[:], scalar=rstd0[:], in1=var_eps[:],
                                               op0=ALU.mult, op1=ALU.mult))
                chain(dve.tensor_scalar(newton2[:], newton[:], -0.5, 1.5, ALU.mult, ALU.add))
                chain(dve.tensor_tensor(rstd[:], newton2[:], rstd0[:], ALU.mult))
                dve.scalar_tensor_tensor(out=h_buf[:, t, :], in0=h_buf[:, t, :], scalar=rstd[:],
                                         in1=beta[:], op0=ALU.mult, op1=ALU.add).then_inc(ln_done, 1)

            def mem_probs(g):
                ch, t = divmod(g - 2 * NT, NT)
                dst = p_store[:, t, :] if ch == 0 else p_work[t % 2][:]
                emptied(dve, l_free, L_GEMM + g)
                if g > 2 * NT:
                    dve.wait_ge(mem_prob_done, g - 2 * NT)
                chain(dve.reciprocal(mem_inv[:], mem_sum[g % 2][:]))
                view = dst.rearrange("p (h m) -> p h m", h=2)
                dve.tensor_tensor(view, view, mem_inv[:].rearrange("p (h o) -> p h o", o=1)
                                  .to_broadcast([P, 2, MEM]), ALU.mult).then_inc(mem_prob_done, 1)

            low_groups(T_O, 0, 0)
            low_groups(T_O + 2, 1, 2)
            for g in range(N_GEMM + 2):
                stage, ch, t = g // (2 * NT), g // NT % 2, g % NT
                n = L_GEMM + g
                col = slice(ch * HALF, (ch + 1) * HALF)
                if g < N_GEMM:
                    filled(dve, l_full, n)
                if stage == 0:
                    dve.wait_ge(x_res_in[g % 2], 16 * (g // 2 + 1))
                    dve.scalar_tensor_tensor(out=h_buf[:, t, col], in0=x_res[g % 2][:], scalar=ALPHA,
                                             in1=ring_l[n % 2][:, 0:HALF], op0=ALU.mult, op1=ALU.add)\
                        .then_inc(l_free[n % 2], 1)
                elif stage == 1:
                    if g >= 2 * NT + 2:
                        dve.wait_ge(mem_bias_done, g - 2 * NT - 1)
                    chain(dve.tensor_reduce(mem_max[g % 2][:],
                                            ring_l[n % 2][:, 0:HALF].rearrange("p (h m) -> p h m", h=2),
                                            AX.X, ALU.max))
                    dve.tensor_scalar(mem_bias[g % 2][:], mem_max[g % 2][:], -MEM_SCALE, None, ALU.mult)\
                        .then_inc(mem_bias_done, 1)
                elif stage == 2:
                    dve.wait_ge(ln_done, t + 1)
                    dve.scalar_tensor_tensor(out=h_buf[:, t, col], in0=h_buf[:, t, col], scalar=ALPHA,
                                             in1=ring_l[n % 2][:, 0:HALF], op0=ALU.mult, op1=ALU.add)\
                        .then_inc(l_free[n % 2], 1)
                if stage in (0, 2) and ch == 1:
                    emptied(dve, l_free, n)
                    moments(stage // 2 * NT + t, t)
                if g + 2 < NT:
                    low_groups(T_O + 2 * (g + 2), g + 2, 2 * (g + 2))
                before = g - 1
                if before >= 0:
                    bs, bch, bt = before // (2 * NT), before // NT % 2, before % NT
                    if bs == 1:
                        mem_probs(before)
                    elif bs in (0, 2) and bch == 1:
                        norm(bs // 2 * NT + bt, bt)
                if transposed_at(g):
                    s, tt = transposed_at(g)
                    low_groups(T_STAGE + 2 * (s * NT + tt), tt, 2 * NT + 2 * (s * NT + tt))

            def square(u):
                for j in range(2):
                    q = 2 * u + j
                    emptied(dve, a_free, A_UP + q)
                    dve.tensor_tensor(relu_buf[q % 2][:], relu_buf[q % 2][:], relu_buf[q % 2][:], ALU.mult)\
                        .then_inc(sq_done, 1)
                for j in range(2):
                    q = 2 * u + j
                    dve.wait_ge(hid_hi_done, q + 1)
                    dve.tensor_tensor(hid_lo[u % 2][:, j, :], relu_buf[q % 2][:],
                                      hid_hi[u % 2][:, j, :].bitcast(F32), ALU.subtract)\
                        .then_inc(hid_ready, 1)

            square(0)
            for u in range(2 * N_FF):
                if u + 1 < 2 * N_FF:
                    square(u + 1)
                f, hf = divmod(u, 2)
                for tt in range(4):
                    t = 4 * hf + tt
                    n = L_DOWN + 4 * u + tt
                    filled(dve, l_full, n)
                    if f == 0:
                        dve.wait_ge(ln_done, NT + t + 1)
                        dve.scalar_tensor_tensor(out=h_buf[:, t, :], in0=h_buf[:, t, :], scalar=ALPHA,
                                                 in1=ring_l[n % 2][:], op0=ALU.mult, op1=ALU.add)\
                            .then_inc(l_free[n % 2], 1)
                    else:
                        emptied(dve, l_free, n - 8)
                        dve.tensor_tensor(h_buf[:, t, :], h_buf[:, t, :], ring_l[n % 2][:], ALU.add)\
                            .then_inc(l_free[n % 2], 1)
                    if f == N_FF - 1:
                        emptied(dve, l_free, n)
                        moments(2 * NT + t, t)
                        if t:
                            norm(2 * NT + t - 1, t - 1)
            norm(3 * NT - 1, NT - 1)


INPUTS = ("x", "x_t", "mem_t", "positions", "w_v", "w_k", "w_iq", "w_dq", "w_sq", "bias_qk", "bias_v", "sinks",
          "wk_mem", "wv_mem", "wq_mem", "wo_mem", "w_o", "w_up", "w_down", "gamma", "beta",
          "ident", "rot", "swa_mask", "causal", "inv_freq")


def k_tiles(w):
    return np.ascontiguousarray(w.reshape(-1, P, w.shape[1]).transpose(1, 0, 2))


def lay_out(x, mem, positions, w_in, b_in, swa_sinks, w_o, ln1_g, ln1_b, wq_mem, wk_mem, wv_mem, wo_mem,
            ln2_g, ln2_b, w_up, w_down, ln3_g, ln3_b):
    g = {}
    g["x"] = x[0].reshape(NT, P, D)
    g["x_t"] = x[0].T.reshape(NK, P, SEQ)
    g["mem_t"] = k_tiles(mem[0].T)
    g["positions"] = positions[0]
    at = np.cumsum([0, HEADS * HEAD, HEAD, HEAD, HEADS * HEAD, HEAD, HEADS, HEADS * HEAD, 2 * HEAD, 2 * HEAD])
    w, b = w_in[0], b_in[0]
    names = ("dq", "dk", "dv", "iq", "ik", "iw", "sq", "sk", "sv")
    part = {n: (w[:, at[i]:at[i + 1]], b[at[i]:at[i + 1]]) for i, n in enumerate(names)}
    g["w_v"] = k_tiles(np.concatenate([part[n][0] for n in ("iw", "dv", "sv")], axis=1)).reshape(P, -1)
    g["bias_v"] = np.concatenate([part[n][1] for n in ("iw", "dv", "sv")])
    g["w_k"] = k_tiles(np.concatenate([part[n][0] for n in ("dk", "ik", "sk")], axis=1)).reshape(P, -1)
    for n in ("iq", "dq", "sq"):
        g[f"w_{n}"] = np.stack([k_tiles(part[n][0][:, c:c + 256]).reshape(P, -1) for c in (0, 256)])
    g["bias_qk"] = np.concatenate([part[n][1] for n in ("dk", "ik", "sk", "iq", "dq", "sq")]).reshape(14, P).T
    g["sinks"] = swa_sinks[0]
    head = lambda w, h: w[:, h * MEM_HEAD:(h + 1) * MEM_HEAD]
    heads = range(MEM_HEADS)
    g["wk_mem"] = np.stack([k_tiles(head(wk_mem[0], h)).reshape(P, -1) for h in heads])
    g["wv_mem"] = np.stack([k_tiles(head(wv_mem[0], h)).reshape(P, -1) for h in heads])
    g["wq_mem"] = np.stack([k_tiles(head(wq_mem[0], h).T).reshape(P, -1) for h in heads])
    g["wo_mem"] = np.stack([k_tiles(wo_mem[0][h * MEM_HEAD:(h + 1) * MEM_HEAD]).reshape(P, -1) for h in heads])
    g["w_o"] = np.stack([k_tiles(w_o[0][kh * HALF:(kh + 1) * HALF, ch * HALF:(ch + 1) * HALF]).reshape(P, -1)
                         for ch in range(2) for kh in range(2)])
    g["w_up"] = np.stack([k_tiles(w_up[0][:, f * 256:(f + 1) * 256]).reshape(P, -1) for f in range(N_FF)])
    g["w_down"] = np.stack([k_tiles(w_down[0][f * 256:(f + 1) * 256]).reshape(P, -1) for f in range(N_FF)])
    g["gamma"] = np.stack([ln1_g[0], ln2_g[0], ln3_g[0]])
    g["beta"] = np.stack([ln1_b[0], ln2_b[0], ln3_b[0]])

    g["ident"] = np.eye(P, dtype=np.float32)
    rot = np.zeros((P, P), np.float32)
    for m in range(P):
        d = m % HEAD
        rot[m + HEAD // 2 if d < HEAD // 2 else m - HEAD // 2, m] = -1.0 if d < HEAD // 2 else 1.0
    g["rot"] = rot
    q, k = np.arange(P)[:, None], np.arange(P)[None, :]
    own = np.where(k <= q, 0.0, MASKED)
    g["swa_mask"] = np.concatenate([np.where(k > q, 0.0, MASKED), own], axis=1).astype(np.float32)
    g["causal"] = np.concatenate([np.zeros((P, P)), own], axis=1).astype(np.float32)
    inv = (10000.0 ** (-np.arange(0, HEAD, 2, dtype=np.float64) / HEAD)).astype(np.float32)
    g["inv_freq"] = np.tile(inv, P // (HEAD // 2)).reshape(P, 1)
    return {n: np.ascontiguousarray(g[n]) for n in INPUTS}


def kernel(**inputs):
    import concourse.bacc as bacc
    from concourse.bass_utils import run_bass_kernel_spmd

    nc = bacc.Bacc("TRN2", target_bir_lowering=False, num_devices=1)
    arrays, aps = {}, {}
    for name, array in lay_out(**{n: np.asarray(v) for n, v in inputs.items()}).items():
        arrays[f"{name}_dram"] = array
        aps[name] = nc.dram_tensor(f"{name}_dram", array.shape, mybir.dt.from_np(array.dtype),
                                   kind="ExternalInput").ap()
    aps["out"] = nc.dram_tensor("out_dram", (NT, P, D), F32, kind="ExternalOutput").ap()
    build_layer(nc, aps)
    result = run_bass_kernel_spmd(nc, [arrays], core_ids=[0])
    return result.results[0]["out_dram"].reshape(1, SEQ, D)
```
